# Optimizing a Trainium2 kernel written in Bass

```python
import jax, jax.numpy as jnp
from jax import lax
import numpy as np

D_MODEL = 1024
BATCH = 1
SEQ = 256
DEPTH = 2

CTX_LEN = 256
GRID_W = 64
N_EVEN = (DEPTH + 1) // 2
N_ODD = DEPTH // 2
EPS = 1e-6

LRU_WIDTH = D_MODEL
LRU_BLOCKS = 16
LRU_BLOCK = LRU_WIDTH // LRU_BLOCKS
LRU_C = 8.0
CONV_WIDTH = 4
CONV_LEFT = 2
DN_HEADS = 8
DN_DK = 128
DN_DV = 128
DN_CHUNK = 64
DN_QKV = DN_HEADS * (2 * DN_DK + DN_DV)
GATE_COL_SCALE = 0.1
EVEN_SPLITS = [LRU_WIDTH, 2 * LRU_WIDTH, 2 * LRU_WIDTH + DN_QKV, 2 * LRU_WIDTH + DN_QKV + DN_HEADS * DN_DV,
               2 * LRU_WIDTH + DN_QKV + DN_HEADS * DN_DV + 2 * DN_HEADS]
EVEN_IN_COLS = 2 * LRU_WIDTH + DN_QKV + DN_HEADS * DN_DV + 4 * DN_HEADS
EVEN_MIX = LRU_WIDTH + DN_HEADS * DN_DV
N_Q_HEADS = 8
N_KV_HEADS = 4
Q_PER_KV = N_Q_HEADS // N_KV_HEADS
HEAD_DIM = 128
ROPE_AXIS_DIM = HEAD_DIM // 2
ROPE_THETA = 10000.0
Q_BLOCK = 128
ATT_COLS = (N_Q_HEADS + 2 * N_KV_HEADS) * HEAD_DIM
D_FF = 4 * D_MODEL

kernel_name = 'hybrid_rglru_gdn_gqa_prefix_dit'

F32 = jnp.float32

def rms_norm(x, g):
    xf = x.astype(F32)
    y = xf * lax.rsqrt(jnp.mean(xf * xf, axis=-1, keepdims=True) + EPS)
    return (y * g.astype(F32)).astype(x.dtype)

def l2_normalize(x):
    xf = x.astype(F32)
    return xf * lax.rsqrt(jnp.sum(xf * xf, axis=-1, keepdims=True) + EPS)

def dw_conv(x, w, b=None):
    L = x.shape[1]
    xp = jnp.pad(x, ((0, 0), (CONV_LEFT, CONV_WIDTH - 1 - CONV_LEFT), (0, 0)))
    y = xp[:, 0:L] * w[0]
    for j in range(1, CONV_WIDTH):
        y = y + xp[:, j:j + L] * w[j]
    return y if b is None else y + b

def sq_relu_mlp(h, w1, w2):
    return jnp.square(jax.nn.relu(h @ w1)) @ w2

def lru_gates(xc, w_a, b_a, w_i, b_i, lam):
    xf = xc.astype(F32)
    xb = xf.reshape(*xf.shape[:-1], LRU_BLOCKS, LRU_BLOCK)
    r = jax.nn.sigmoid(jnp.einsum('blnj,njk->blnk', xb, w_a.astype(F32)).reshape(xf.shape) + b_a.astype(F32))
    i = jax.nn.sigmoid(jnp.einsum('blnj,njk->blnk', xb, w_i.astype(F32)).reshape(xf.shape) + b_i.astype(F32))
    log_a = -LRU_C * r * jax.nn.softplus(-lam.astype(F32))
    a = jnp.exp(log_a)
    b = jnp.sqrt(-jnp.expm1(2.0 * log_a)) * (i * xf)
    return a, b

def linear_scan(a, b, h0, reverse):
    def combine(e1, e2):
        a1, b1 = e1
        a2, b2 = e2
        return a1 * a2, a2 * b1 + b2
    a_cum, b_cum = lax.associative_scan(combine, (a, b), axis=1, reverse=reverse)
    return b_cum if h0 is None else a_cum * h0[:, None] + b_cum

def delta_chunked(q, k, v, beta, g, s0):
    bsz, L, H, dk = q.shape
    dv = v.shape[-1]
    n = L // DN_CHUNK

    def to_chunks(t):
        return jnp.transpose(t.reshape(bsz, n, DN_CHUNK, H, -1), (1, 0, 3, 2, 4))

    qc, kc, vc = to_chunks(q), to_chunks(k), to_chunks(v)
    bc = to_chunks(beta[..., None])[..., 0]
    gcum = jnp.cumsum(to_chunks(g[..., None])[..., 0], axis=-1)
    idx = jnp.arange(DN_CHUNK)
    causal = idx[:, None] >= idx[None, :]
    strict = idx[:, None] > idx[None, :]
    decay = jnp.exp(jnp.where(causal, gcum[..., :, None] - gcum[..., None, :], -jnp.inf))
    k_beta = kc * bc[..., None]
    m = jnp.where(strict, jnp.einsum('nbhid,nbhjd->nbhij', k_beta, kc) * decay, 0.0)
    eye = jnp.eye(DN_CHUNK, dtype=F32)
    rhs = jnp.concatenate([vc * bc[..., None], k_beta * jnp.exp(gcum)[..., None]], axis=-1)
    sol = lax.linalg.triangular_solve(eye + m, rhs, left_side=True, lower=True, unit_diagonal=True)
    u, w = sol[..., :dv], sol[..., dv:]
    attn = jnp.einsum('nbhid,nbhjd->nbhij', qc, kc) * decay
    q_dec = qc * jnp.exp(gcum)[..., None]
    g_last = gcum[..., -1]
    k_dec = kc * jnp.exp(g_last[..., None] - gcum)[..., None]

    def step(S, xs):
        u_i, w_i, q_i, k_i, attn_i, gl = xs
        v_new = u_i - jnp.einsum('bhck,bhkv->bhcv', w_i, S)
        o = jnp.einsum('bhck,bhkv->bhcv', q_i, S) + jnp.einsum('bhij,bhjv->bhiv', attn_i, v_new)
        S = S * jnp.exp(gl)[..., None, None] + jnp.einsum('bhck,bhcv->bhkv', k_i, v_new)
        return S, o

    S, o = lax.scan(step, s0, (u, w, q_dec, k_dec, attn, g_last))
    o = jnp.transpose(o, (1, 0, 3, 2, 4)).reshape(bsz, L, H, dv)
    return o, S

def even_mixer(hc, hx, w_in, lru_cw, lru_cb, lru_wa, lru_ba, lru_wi, lru_bi, lru_lam,
               dn_cw, dn_alog, dn_dtb, dn_g, w_out, with_ctx_out):
    def prep(h):
        bsz, L, _ = h.shape
        xr, yr, qkv, z, beta_raw, alpha_raw = jnp.split(h @ w_in, EVEN_SPLITS, axis=-1)
        xr = dw_conv(xr, lru_cw, lru_cb)
        q, k, v = jnp.split(jax.nn.silu(dw_conv(qkv, dn_cw)), [DN_HEADS * DN_DK, 2 * DN_HEADS * DN_DK], axis=-1)
        q = l2_normalize(q.reshape(bsz, L, DN_HEADS, DN_DK)) * (DN_DK ** -0.5)
        k = l2_normalize(k.reshape(bsz, L, DN_HEADS, DN_DK))
        v = v.reshape(bsz, L, DN_HEADS, DN_DV).astype(F32)
        beta = jax.nn.sigmoid(beta_raw.astype(F32)).reshape(bsz, L, 2, DN_HEADS)
        g = -jnp.exp(dn_alog.astype(F32)) * jax.nn.softplus(
            alpha_raw.astype(F32).reshape(bsz, L, 2, DN_HEADS) + dn_dtb.astype(F32))
        return xr, yr, q, k, v, z, beta, g

    xr_c, yr_c, q_c, k_c, v_c, z_c, beta_c, g_c = prep(hc)
    xr_x, yr_x, q_x, k_x, v_x, z_x, beta_x, g_x = prep(hx)
    s0 = jnp.zeros((hx.shape[0], DN_HEADS, DN_DK, DN_DV), F32)
    lru_c, lru_x, dn_c, dn_x = [], [], [], []
    for d, rev in enumerate((False, True)):
        flip = (lambda t: jnp.flip(t, axis=1)) if rev else (lambda t: t)
        a_c, b_c = lru_gates(xr_c, lru_wa[d], lru_ba[d], lru_wi[d], lru_bi[d], lru_lam[d])
        h_c = linear_scan(a_c, b_c, None, rev)
        a_x, b_x = lru_gates(xr_x, lru_wa[d], lru_ba[d], lru_wi[d], lru_bi[d], lru_lam[d])
        h_x = linear_scan(a_x, b_x, h_c[:, 0] if rev else h_c[:, -1], rev)
        lru_c.append(h_c)
        lru_x.append(h_x)
        o_c, s_c = delta_chunked(flip(q_c), flip(k_c), flip(v_c), flip(beta_c[:, :, d]), flip(g_c[:, :, d]), s0)
        o_x, _ = delta_chunked(flip(q_x), flip(k_x), flip(v_x), flip(beta_x[:, :, d]), flip(g_x[:, :, d]), s_c)
        dn_c.append(flip(o_c))
        dn_x.append(flip(o_x))

    def merge(h_lru, o_dn, yr, z):
        bsz, L, _ = yr.shape
        lru = h_lru.astype(yr.dtype) * jax.nn.gelu(yr)
        dn = rms_norm(o_dn, dn_g).astype(z.dtype) * jax.nn.silu(z.reshape(bsz, L, DN_HEADS, DN_DV))
        return jnp.concatenate([lru, dn.reshape(bsz, L, DN_HEADS * DN_DV)], axis=-1) @ w_out

    ox = merge(lru_x[0] + lru_x[1], dn_x[0] + dn_x[1], yr_x, z_x)
    oc = merge(lru_c[0] + lru_c[1], dn_c[0] + dn_c[1], yr_c, z_c) if with_ctx_out else None
    return oc, ox

def rope_tables(n_tokens):
    rows = n_tokens // GRID_W
    row_id = jnp.repeat(jnp.arange(rows), GRID_W).astype(F32)
    col_id = jnp.tile(jnp.arange(GRID_W), rows).astype(F32)
    inv_freq = ROPE_THETA ** (-jnp.arange(0, ROPE_AXIS_DIM, 2, dtype=F32) / ROPE_AXIS_DIM)
    ang_r = row_id[:, None] * inv_freq[None]
    ang_c = col_id[:, None] * inv_freq[None]
    return jnp.cos(ang_r), jnp.sin(ang_r), jnp.cos(ang_c), jnp.sin(ang_c)

def rope_1d(x, cos, sin):
    half = x.shape[-1] // 2
    x1, x2 = x[..., :half], x[..., half:]
    c, s = cos[None, :, None], sin[None, :, None]
    return jnp.concatenate([x1 * c - x2 * s, x2 * c + x1 * s], axis=-1)

def rope_2d(x, rope):
    cr, sr, cc, sc = rope
    xf = x.astype(F32)
    out = jnp.concatenate([rope_1d(xf[..., :ROPE_AXIS_DIM], cr, sr), rope_1d(xf[..., ROPE_AXIS_DIM:], cc, sc)], axis=-1)
    return out.astype(x.dtype)

def gqa_attend(q, k, v):
    bsz, lq = q.shape[:2]
    qg = q.reshape(bsz, lq, N_KV_HEADS, Q_PER_KV, HEAD_DIM)
    s = jnp.einsum('bqgrd,bkgd->bgrqk', qg, k).astype(F32) * (HEAD_DIM ** -0.5)
    p = jax.nn.softmax(s, axis=-1).astype(v.dtype)
    o = jnp.einsum('bgrqk,bkgd->bqgrd', p, v)
    return o.reshape(bsz, lq, N_Q_HEADS * HEAD_DIM)

def odd_mixer(hc, hx, w_qkv, q_g, k_g, w_o, rope, with_ctx_out):
    def proj(h):
        bsz, L, _ = h.shape
        q, k, v = jnp.split(h @ w_qkv, [N_Q_HEADS * HEAD_DIM, (N_Q_HEADS + N_KV_HEADS) * HEAD_DIM], axis=-1)
        q = rms_norm(q.reshape(bsz, L, N_Q_HEADS, HEAD_DIM), q_g)
        k = rms_norm(k.reshape(bsz, L, N_KV_HEADS, HEAD_DIM), k_g)
        return q, k, v.reshape(bsz, L, N_KV_HEADS, HEAD_DIM)

    q_c, k_c, v_c = proj(hc)
    q_x, k_x, v_x = proj(hx)
    q_x = rope_2d(q_x, rope)
    k_x = rope_2d(k_x, rope)
    k_all = jnp.concatenate([k_c, k_x], axis=1)
    v_all = jnp.concatenate([v_c, v_x], axis=1)
    bsz, L = hx.shape[:2]
    nb = L // Q_BLOCK
    qb = jnp.transpose(q_x.reshape(bsz, nb, Q_BLOCK, N_Q_HEADS, HEAD_DIM), (1, 0, 2, 3, 4))
    ob = lax.map(lambda qi: gqa_attend(qi, k_all, v_all), qb)
    ox = jnp.transpose(ob, (1, 0, 2, 3)).reshape(bsz, L, N_Q_HEADS * HEAD_DIM) @ w_o
    oc = gqa_attend(q_c, k_c, v_c) @ w_o if with_ctx_out else None
    return oc, ox

def setup_inputs(seed: int = 0) -> dict:
    key = jax.random.key(seed)
    ks = iter(jax.random.split(key, 32))

    def nrm(shape, scale):
        return scale * jax.random.normal(next(ks), shape, F32)

    def gain(shape):
        return 1.0 + nrm(shape, 0.02)

    D = D_MODEL
    x = nrm((BATCH, SEQ, D), 1.0)
    c = nrm((BATCH, D), 1.0)
    ctx = nrm((BATCH, CTX_LEN, D), 1.0)
    c_ctx = nrm((D,), 1.0)
    norm_mix_g = gain((DEPTH, D))
    norm_mlp_g = gain((DEPTH, D))
    w_mod = nrm((DEPTH, D, 6 * D), 0.5 * D ** -0.5)
    b_mod = nrm((DEPTH, 6 * D), 0.02)
    mlp_w1 = nrm((DEPTH, D, D_FF), D ** -0.5)
    mlp_w2 = nrm((DEPTH, D_FF, D), D_FF ** -0.5)
    col_scale = jnp.concatenate([jnp.ones((EVEN_IN_COLS - 4 * DN_HEADS,), F32),
                                 jnp.full((4 * DN_HEADS,), GATE_COL_SCALE, F32)])
    even_w_in = nrm((N_EVEN, D, EVEN_IN_COLS), D ** -0.5) * col_scale
    lru_conv_w = nrm((N_EVEN, CONV_WIDTH, LRU_WIDTH), CONV_WIDTH ** -0.5)
    lru_conv_b = nrm((N_EVEN, LRU_WIDTH), 0.02)
    lru_w_a = nrm((N_EVEN, 2, LRU_BLOCKS, LRU_BLOCK, LRU_BLOCK), LRU_BLOCK ** -0.5)
    lru_b_a = nrm((N_EVEN, 2, LRU_WIDTH), 0.02)
    lru_w_i = nrm((N_EVEN, 2, LRU_BLOCKS, LRU_BLOCK, LRU_BLOCK), LRU_BLOCK ** -0.5)
    lru_b_i = nrm((N_EVEN, 2, LRU_WIDTH), 0.02)
    a_pow = jax.random.uniform(next(ks), (N_EVEN, 2, LRU_WIDTH), F32, minval=0.9, maxval=0.999)
    a0 = a_pow ** (1.0 / LRU_C)
    lru_lambda = jnp.log(a0) - jnp.log1p(-a0)
    dn_conv_w = nrm((N_EVEN, CONV_WIDTH, DN_QKV), CONV_WIDTH ** -0.5)
    dn_a_log = jnp.log(jax.random.uniform(next(ks), (N_EVEN, 2, DN_HEADS), F32, minval=1.0, maxval=16.0))
    dt = jnp.exp(jax.random.uniform(next(ks), (N_EVEN, 2, DN_HEADS), F32,
                                    minval=float(np.log(0.001)), maxval=float(np.log(0.1))))
    dn_dt_bias = dt + jnp.log(-jnp.expm1(-dt))
    dn_norm_g = gain((N_EVEN, DN_DV))
    even_w_out = nrm((N_EVEN, EVEN_MIX, D), EVEN_MIX ** -0.5)
    attn_w_qkv = nrm((N_ODD, D, ATT_COLS), D ** -0.5)
    attn_q_norm_g = gain((N_ODD, HEAD_DIM))
    attn_k_norm_g = gain((N_ODD, HEAD_DIM))
    attn_w_o = nrm((N_ODD, N_Q_HEADS * HEAD_DIM, D), (N_Q_HEADS * HEAD_DIM) ** -0.5)
    final_norm_g = gain((D,))
    return {'x': x, 'c': c, 'ctx': ctx, 'c_ctx': c_ctx, 'norm_mix_g': norm_mix_g, 'norm_mlp_g': norm_mlp_g,
            'w_mod': w_mod, 'b_mod': b_mod, 'mlp_w1': mlp_w1, 'mlp_w2': mlp_w2, 'even_w_in': even_w_in,
            'lru_conv_w': lru_conv_w, 'lru_conv_b': lru_conv_b, 'lru_w_a': lru_w_a, 'lru_b_a': lru_b_a,
            'lru_w_i': lru_w_i, 'lru_b_i': lru_b_i, 'lru_lambda': lru_lambda, 'dn_conv_w': dn_conv_w,
            'dn_a_log': dn_a_log, 'dn_dt_bias': dn_dt_bias, 'dn_norm_g': dn_norm_g, 'even_w_out': even_w_out,
            'attn_w_qkv': attn_w_qkv, 'attn_q_norm_g': attn_q_norm_g, 'attn_k_norm_g': attn_k_norm_g,
            'attn_w_o': attn_w_o, 'final_norm_g': final_norm_g}

def reference(x, c, ctx, c_ctx, norm_mix_g, norm_mlp_g, w_mod, b_mod, mlp_w1, mlp_w2, even_w_in,
              lru_conv_w, lru_conv_b, lru_w_a, lru_b_a, lru_w_i, lru_b_i, lru_lambda, dn_conv_w,
              dn_a_log, dn_dt_bias, dn_norm_g, even_w_out, attn_w_qkv, attn_q_norm_g, attn_k_norm_g,
              attn_w_o, final_norm_g):
    rope = rope_tables(x.shape[1])
    xs, cs = x, ctx
    for l in range(DEPTH):
        last = l == DEPTH - 1
        j = l // 2
        mod_x = (jax.nn.silu(c) @ w_mod[l] + b_mod[l])[:, None, :]
        mod_c = (jax.nn.silu(c_ctx) @ w_mod[l] + b_mod[l])[None, None, :]
        sh1, sc1, g1, sh2, sc2, g2 = jnp.split(mod_x, 6, axis=-1)
        csh1, csc1, cg1, csh2, csc2, cg2 = jnp.split(mod_c, 6, axis=-1)
        hx = rms_norm(xs, norm_mix_g[l]) * (1 + sc1) + sh1
        hc = rms_norm(cs, norm_mix_g[l]) * (1 + csc1) + csh1
        if l % 2 == 0:
            oc, ox = even_mixer(hc, hx, even_w_in[j], lru_conv_w[j], lru_conv_b[j], lru_w_a[j], lru_b_a[j],
                                lru_w_i[j], lru_b_i[j], lru_lambda[j], dn_conv_w[j], dn_a_log[j],
                                dn_dt_bias[j], dn_norm_g[j], even_w_out[j], not last)
        else:
            oc, ox = odd_mixer(hc, hx, attn_w_qkv[j], attn_q_norm_g[j], attn_k_norm_g[j], attn_w_o[j],
                               rope, not last)
        xs = xs + g1 * ox
        xs = xs + g2 * sq_relu_mlp(rms_norm(xs, norm_mlp_g[l]) * (1 + sc2) + sh2, mlp_w1[l], mlp_w2[l])
        if not last:
            cs = cs + cg1 * oc
            cs = cs + cg2 * sq_relu_mlp(rms_norm(cs, norm_mlp_g[l]) * (1 + csc2) + csh2, mlp_w1[l], mlp_w2[l])
    return rms_norm(xs, final_norm_g)


_drawn_inputs = setup_inputs


def setup_inputs(seed=0):
    import zlib

    import numpy as np

    out = dict(_drawn_inputs(seed))
    spreads = {}
    factors = {'norm_mix_g': 6.057,
     'norm_mlp_g': 4.66,
     'lru_b_a': 8.0,
     'lru_b_i': 8.0,
     'dn_a_log': 2.714,
     'dn_norm_g': 8.0,
     'attn_q_norm_g': 27.347,
     'attn_k_norm_g': 26.693,
     'final_norm_g': 9.604}
    for name, (base, spread) in spreads.items():
        noise = np.random.default_rng([zlib.crc32(name.encode()), seed]).standard_normal(out[name].shape)
        drawn = base * np.exp(spread * noise) if base else spread * noise
        out[name] = __import__('jax').numpy.asarray(drawn.astype(out[name].dtype))
    for name, factor in factors.items():
        out[name] = (out[name] * factor).astype(out[name].dtype)
    return out
```

```python
from contextlib import ExitStack

import numpy as np

import concourse.bass as bass
from concourse import mybir

F32 = mybir.dt.float32
F32R = mybir.dt.float32r
ACT = mybir.ActivationFunctionType
ALU = mybir.AluOpType
ENG = mybir.EngineType

P = 128
D = 1024
KT = D // P
T = 512
CTX = 256
NT = T // P
EPS = 1e-6
HEADS = 8
GRID_W = 64
LRU_C = 8.0
SEGS = ((0, 0, CTX), (1, CTX, T))
UNIT_K, UNIT_C = 4, 256
RAW, SPLIT = 4, 2
MOD_BATCH, MOD_ALL = 8, 48
PRIME_SPLIT, PRIME_EVAC, PRIME_SLOT, PRIME_MOD, PRIME_HID = 4, 4, 2, 4, 4

CONST_AT = {}


def make_consts():
    i = np.arange(P)
    row, col = i[:, None], i[None, :]
    parts = [("ident", row == col), ("ones", np.ones((P, P))), ("le", row <= col), ("ge", row >= col),
             ("gt", row > col), ("lt", row < col)]
    parts += [("pair_f", (row // 2 == col // 2) & (row < col)), ("pair_r", (row // 2 == col // 2) & (row > col))]
    c = np.arange(P // 2)[None, :]
    for s in (2, 4, 8, 16, 32, 64):
        r = row - 2 * s * (c // s)
        parts.append((f"m{s}_f", (r >= s) & (r < 2 * s)))
        parts.append((f"m{s}_r", (r >= 0) & (r < s)))
    half = P // 4
    inv = 10000.0 ** (-np.arange(0, P // 2, 2, dtype=np.float32) / np.float32(P // 2))
    tok = np.arange(T - CTX)
    pos = np.where((i < P // 2)[:, None], (tok // GRID_W)[None, :], (tok % GRID_W)[None, :]).astype(np.float32)
    ang = pos * inv.astype(np.float32)[i % half][:, None]
    rot = np.where((col == row - half) & (col % (2 * half) < half), -1.0, 0.0) + \
        np.where((col == row + half) & (col % (2 * half) >= half), 1.0, 0.0)
    parts.append(("rot", rot))
    parts += [("eps", np.full((P, 1), EPS)), ("pad", np.zeros((P, 7)))]
    parts += [("cos", np.cos(ang)), ("sin", np.sin(ang))]
    at, arrays = 0, []
    for name, a in parts:
        CONST_AT[name] = (at, at + a.shape[1])
        at += a.shape[1]
        arrays.append(np.asarray(a, np.float32))
    return np.ascontiguousarray(np.concatenate(arrays, 1))


CONSTS = make_consts()
NCONST = CONSTS.shape[1]
N_EARLY = CONST_AT["cos"][0]

VEC, _at = {}, 0
for _name, _n in (("c_ctx", 8), ("c", 8), ("mix_g", 16), ("mlp_g", 16), ("conv_w", 32), ("conv_b", 8),
                  ("b_a", 16), ("b_i", 16), ("final_g", 8),
                  ("b_mod", 96), ("lam", 16), ("dn_g", 1), ("q_g", 1), ("k_g", 1), ("pad", 13),
                  ("dn_conv", 96)):
    VEC[_name] = _at
    _at += _n
NVEC = _at
VEC_B, VEC_C = VEC["b_mod"], VEC["dn_conv"]
VEC_B_ROWS = VEC["pad"] - VEC["b_mod"]

def segments():
    segs = [("xr", "w_in", 0, 8, 0, 2), ("qkv", "w_in", 2048, 8, 0, 6), ("z", "w_in", 5120, 8, 0, 2),
            ("yr", "w_in", 1024, 8, 0, 2), ("out", "w_out", 0, 16, 0, 2)]
    for l in (0, 1):
        if l == 1:
            segs += [("q", "w_qkv", 0, 8, 0, 2), ("k", "w_qkv", 1024, 8, 0, 1),
                     ("v", "w_qkv", 1536, 8, 0, 1), ("wo", "w_o", 0, 8, 0, 2)]
        for half in (0, 1):
            segs.append((f"up{l}{half}", f"w1_{l}", 2048 * half, 8, 0, 4))
            segs.append((f"down{l}{half}", f"w2_{l}", 0, 16, 16 * half, 2))
    return segs


SEG = {}
ORDER = []


def plan():
    unit = pair = up = 0
    for name, w, c0, kt, kr, bodies in segments():
        s = dict(name=name, w=w, c0=c0, kt=kt, kr=kr, bodies=bodies, unit=unit, pair=pair, upp=kt // UNIT_K, up=up)
        SEG[name] = s
        ORDER.append(s)
        unit += bodies * 2 * s["upp"]
        pair += bodies * 2
        if name.startswith("up"):
            up += bodies * 4


plan()


def build(nc, a, out):
    ctx = ExitStack()
    with ctx:
        sems = {}

        def sem(name):
            sems[name] = ctx.enter_context(nc.semaphore(name))
            return sems[name]

        base = [(nc.sbuf_base + 31) // 32 * 32]

        def at(name, offset, shape, dt=F32):
            return nc.alloc_sbuf_tensor_at(name, [P] + list(shape), dt, offset=offset)

        def place(name, shape, dt=F32):
            size = 4 * int(np.prod(shape))
            t = at(name, base[0], shape, dt)
            base[0] += (size + 31) // 32 * 32
            return t

        cst = place("cst", [NCONST])
        mod_row = at("mod_row", (nc.sbuf_base + 31) // 32 * 32 + 4 * N_EARLY, [2 * UNIT_C])
        vec = place("vec", [NVEC])
        xT = place("xT", [KT, T])
        raw = place("raw", [RAW, UNIT_K, UNIT_C])
        w_hi = place("w_hi", [SPLIT, UNIT_K, UNIT_C], F32R)
        w_lo = place("w_lo", [SPLIT, UNIT_K, UNIT_C], F32R)
        modv = place("modv", [2, 6, 8, 2])
        gain = place("gain", [2, 2, 8, 2])
        cs = place("cs", [8, 32])
        beta = place("beta", [NT, 16])
        gate_raw = place("gate_raw", [NT, 32])
        g_log = place("g_log", [NT, 16])
        neg_eg = place("neg_eg", [NT, 16])
        e_rest = place("e_rest", [NT, 16])
        sp_n = 80
        sp_x = place("sp_x", [sp_n])
        sp_a = place("sp_a", [sp_n])
        sp_b = place("sp_b", [sp_n])
        sp_p = place("sp_p", [sp_n])
        gate_bias = place("gate_bias", [2, 16])
        lru_c = sp_x[:, 64:80]
        mod_off = base[0]
        base[0] += 16384
        free = base[0]
        KB = 1024

        def F(name, kb, shape, dt=F32):
            return at(name, free + int(kb * KB), shape, dt)

        qkv = F("qkv", 0, [24, T])
        xc = F("xc", 48, [8, T])
        siluz = F("siluz", 64, [8, T])
        gy = F("gy", 80, [8, T])
        h_hi = F("h_hi", 96, [KT, T], F32R)
        h_lo = F("h_lo", 112, [KT, T], F32R)
        assert free + 128 * KB <= nc.sbuf_usable_end
        xin = F("xin", 32, [NT, D])
        rowsA = F("rowsA", 48, [P])
        rowsB = F("rowsB", 48.5, [P])
        rowsC = F("rowsC", 49, [P])
        wg = F("wg", 64, [8, 32])
        wg_hi = F("wg_hi", 65, [8, 32], F32R)
        wg_lo = F("wg_lo", 66, [8, 32], F32R)
        n_sq = F("n_sq", 112, [KT, T])
        n_t = F("n_t", 72, [4, T])
        n_rt = F("n_rt", 84, [T])
        n_rs = F("n_rs", 86, [T])
        relu = F("relu", 64, [4, T])
        hid_hi = F("hid_hi", 0, [16, T], F32R)
        hid_lo = F("hid_lo", 32, [16, T], F32R)
        mix_hi = F("mix_hi", 0, [16, T], F32R)
        mix_lo = F("mix_lo", 80, [16, T], F32R)
        d_n = F("d_n", 80, [2, 4, P])
        d_t = F("d_t", 84, [2, 4, P])
        d_tt = F("d_tt", 88, [2, 4, P])
        d_at = F("d_at", 92, [2, 4, P])
        d_gu = F("d_gu", 96, [2, 4, P])
        d_vd = F("d_vd", 96, [2, 4, P])
        d_dt = F("d_dt", 100, [2, 4, P])
        d_vn = F("d_vn", 100, [2, 4, P])
        d_eg = F("d_eg", 104, [2, 4, P])
        d_qd = F("d_qd", 108, [2, 4, P])
        d_s = F("d_s", 112, [2, 4, P])
        d_r = F("d_r", 116, [2, 4, P])
        d_pc = F("d_pc", 120, [2, 4, P // 2])
        sq2 = F("sq2", 112, [2, T])
        rt2 = F("rt2", 116, [2, T])
        rs2 = F("rs2", 120, [2, T])
        k_tok = at("k_tok", mod_off + 8192, [2, 4, P])
        v_tok = at("v_tok", mod_off + 8192 + 4096, [2, 4, P])
        q1 = F("q1", 0, [8, T - CTX])
        k1 = F("k1", 8, [4, T])
        v1 = F("v1", 16, [4, T])
        v1_tok = F("v1_tok", 24, [4, NT, P])
        att_hi = F("att_hi", 32, [8, T], F32R)
        att_lo = F("att_lo", 48, [8, T], F32R)
        prob = F("prob", 72, [2, T])
        probT = F("probT", 76, [2, NT, P])
        rope_a = F("rope_a", 80, [2, 2, T - CTX])
        rope_b = F("rope_b", 84, [2, 2, T - CTX])
        smx = F("smx", 88, [3, 16])
        y_out = F("y_out", 0, [KT, T - CTX])
        o_tok = F("o_tok", 8, [2, D])
        lru_w = at("lru_w", mod_off, [4, 8, P])
        l_a = F("l_a", 96, [4, T])
        l_i = F("l_i", 104, [4, T])
        l_t = F("l_t", 112, [4, T])
        l_q = F("l_q", 120, [4, T])

        bank = [ctx.enter_context(nc.psum_tensor(f"bank{i}", [P, 512], F32)) for i in range(8)]
        MODB, X0, X1, X2 = 4, 5, 6, 7

        def C(name):
            lo_, hi_ = CONST_AT[name]
            return cst[:, lo_:hi_]

        def V(name, i=0, n=1):
            return vec[:, VEC[name] + i:VEC[name] + i + n]

        s_in = sem("s_in")
        s_rope = sem("s_rope")
        s_x = sem("s_x")
        s_rows = sem("s_rows")
        s_vec = sem("s_vec")
        s_cs = sem("s_cs")
        s_xps = sem("s_xps")
        s_xa = sem("s_xa")
        s_xd = sem("s_xd")
        raw_in = [sem(f"raw_in{i}") for i in range(RAW)]
        mod_in = [sem(f"mod_in{i}") for i in range(RAW)]
        hi_ready = sem("hi_ready")
        split_done = sem("split_done")
        slot_free = sem("slot_free")
        evac_done = sem("evac_done")
        act_evac = sem("act_evac")
        mod_used = sem("mod_used")
        mod_rows = sem("mod_rows")
        mod_t = sem("mod_t")
        s_mod = sem("s_mod")
        act_waits = sem("act_waits")
        tap = sem("tap")
        conv_step = sem("conv_step")
        link_d = sem("link_d")
        link_a = sem("link_a")
        s_silu = sem("s_silu")
        s_relu = sem("s_relu")
        s_sq = sem("s_sq")
        s_hid = sem("s_hid")
        hid_done = sem("hid_done")
        s_gate = sem("s_gate")
        s_gps = sem("s_gps")
        s_lin = sem("s_lin")
        s_lzero = sem("s_lzero")
        s_lps = sem("s_lps")
        l_sig = sem("l_sig")
        l_exp = sem("l_exp")
        l_w = sem("l_w")
        l_sqrt = sem("l_sqrt")
        l_out = sem("l_out")
        l2 = {x: sem(f"l2_{x}") for x in ("sq", "ss", "rs", "out")}
        dnn = {x: sem(f"dnn_{x}") for x in ("sq", "ss", "rs", "out")}
        qkn = {x: sem(f"qkn_{x}") for x in ("sq", "ss", "rs", "out")}
        s_mix_hi = sem("s_mix_hi")
        s_mix_lo = sem("s_mix_lo")
        p_tok, a_tok = sem("p_tok"), sem("a_tok")
        v_gu = sem("v_gu")
        p_dt, a_dt = sem("p_dt"), sem("a_dt")
        p_kk = sem("p_kk")
        v_n = sem("v_n")
        v_tt = sem("v_tt")
        p_x1, a_t1 = sem("p_x1"), sem("a_t1")
        v_at = sem("v_at")
        p_ks = sem("p_ks")
        v_r = sem("v_r")
        p_p, v_pc = sem("p_p"), sem("v_pc")
        p_tp, v_t = sem("p_tp"), sem("v_t")
        p_x, a_tt = sem("p_x"), sem("a_tt")
        p_vn, v_vn, v_vd = sem("p_vn"), sem("v_vn"), sem("v_vd")
        p_o, a_o, v_o = sem("p_o"), sem("a_o"), sem("v_o")
        p_s, v_s = sem("p_s"), sem("v_s")
        v_s0 = sem("v_s0")
        p_rot, v_rope = sem("p_rot"), sem("v_rope")
        p_v1, a_v1 = sem("p_v1"), sem("a_v1")
        p_sc, v_mx, a_ex, v_pr = sem("p_sc"), sem("v_mx"), sem("a_ex"), sem("v_pr")
        p_pt, a_pt, p_pv, a_ah, v_al = sem("p_pt"), sem("a_pt"), sem("p_pv"), sem("a_ah"), sem("v_al")
        v_y, p_y, a_y, s_out = sem("v_y"), sem("p_y"), sem("a_y"), sem("s_out")
        norm_sems = {}
        for n in ("mix0", "mlp0", "mix1", "mlp1", "fin"):
            norm_sems[n] = {x: sem(f"{n}_{x}") for x in ("sq", "ss", "rt", "t", "hi", "lo")}
        dcount = [0]
        acount = [0]

        STEPS = [(hg, st, (st, (1, 0, 3, 2)[st])) for hg in range(2) for st in range(4)]
        MOD_TURN = {2: 3, 5: 4}
        LEVELS = (2, 4, 8, 16, 32, 64)
        BA, BB, BC = (0, 2), (1, 3), (X0, X1)

        def lev(ss, l, g):
            return (ss * len(LEVELS) + l) * 2 + g + 1

        def half_cols(buf, g, a_, s_):
            v_ = buf[:, g, a_] if a_ is not None else buf[:, g]
            if a_ is None:
                return v_.rearrange("p a (b two s) -> p (a b) two s", two=2, s=s_)[:, :, g]
            return v_.rearrange("p (b two s) -> p b two s", two=2, s=s_)[:, :, g]

        block = ctx.enter_context(nc.Block())
        w_dram = {"w_in": a["even_w_in"][0], "w_out": a["even_w_out"][0], "w_qkv": a["attn_w_qkv"][0], "w_o": a["attn_w_o"][0],
                  "w1_0": a["mlp_w1"][0], "w1_1": a["mlp_w1"][1], "w2_0": a["mlp_w2"][0], "w2_1": a["mlp_w2"][1]}

        @block.sync
        def _(sp):
            def rows(dst, r0, src, n):
                sp.dma_start(dst[r0:r0 + n, :], src).then_inc(s_in, 16)

            def row_view(name, pat):
                return a[name].rearrange(pat, p=P)

            rows(rowsA, VEC["c_ctx"], a["c_ctx"].rearrange("(k p) -> k p", p=P), 8)
            rows(rowsA, VEC["c"], row_view("c", "a (k p) -> (a k) p"), 8)
            rows(rowsA, VEC["mix_g"], row_view("norm_mix_g", "a (k p) -> (a k) p"), 16)
            rows(rowsA, VEC["mlp_g"], row_view("norm_mlp_g", "a (k p) -> (a k) p"), 16)
            rows(rowsA, VEC["conv_w"], row_view("lru_conv_w", "a j (k p) -> (a j k) p"), 32)
            rows(rowsA, VEC["conv_b"], row_view("lru_conv_b", "a (k p) -> (a k) p"), 8)
            rows(rowsA, VEC["b_a"], row_view("lru_b_a", "a j (k p) -> (a j k) p"), 16)
            rows(rowsA, VEC["b_i"], row_view("lru_b_i", "a j (k p) -> (a j k) p"), 16)
            rows(rowsA, VEC["final_g"], a["final_norm_g"].rearrange("(k p) -> k p", p=P), 8)
            rows(rowsB, 0, row_view("b_mod", "a (k p) -> (a k) p"), 96)
            rows(rowsB, VEC["lam"] - VEC_B, row_view("lru_lambda", "a j (k p) -> (a j k) p"), 16)
            rows(rowsB, VEC["dn_g"] - VEC_B, a["dn_norm_g"], 1)
            rows(rowsB, VEC["q_g"] - VEC_B, a["attn_q_norm_g"], 1)
            rows(rowsB, VEC["k_g"] - VEC_B, a["attn_k_norm_g"], 1)
            rows(rowsC, 0, row_view("dn_conv_w", "a j (k p) -> (a j k) p"), 96)
            sp.dma_start(gate_bias[:, 0, :], a["dn_dt_bias"].rearrange("a j h -> (a j h)").partition_broadcast(P)).then_inc(s_in, 16)
            sp.dma_start(gate_bias[:, 1, :], a["dn_a_log"].rearrange("a j h -> (a j h)").partition_broadcast(P)).then_inc(s_in, 16)
            sp.dma_start(cst[:, 0:N_EARLY], a["consts"][:, 0:N_EARLY]).then_inc(s_in, 16)
            sp.dma_start(xin[:, 0:2, :], a["ctx"][0].rearrange("(n p) d -> p n d", p=P)).then_inc(s_x, 16)
            sp.dma_start(xin[:, 2:4, :], a["x"][0].rearrange("(n p) d -> p n d", p=P)).then_inc(s_x, 16)
            sp.dma_start(wg[:, :, :], w_dram["w_in"][:, 6144:6176].rearrange("(k p) c -> p k c", p=P)).then_inc(s_x, 16)

            def load_unit(src, u, j, col):
                sp.wait_ge(split_done, u + (1))
                sp.dma_start(raw[:, j], src[:, :, bass.ds(col, UNIT_C)]).then_inc(raw_in[j], 16)

            def load_mod(layer, first, bodies):
                src = a["w_mod"][layer].rearrange("(h k p) c -> h p k c", p=P, k=UNIT_K)
                with nc.Fori(0, bodies, engines=[ENG.SP]) as it:
                    for j in range(RAW):
                        sp.wait_ge(mod_used, it * RAW + (2 * first + j + 1))
                        col = it * (2 * UNIT_C) + (first - layer * MOD_ALL // 2 + j // 2) * UNIT_C
                        sp.dma_start(raw[:, j], src[j % 2][:, :, bass.ds(col, UNIT_C)]).then_inc(mod_in[j], 16)

            load_mod(0, 0, MOD_BATCH // 2)
            sp.wait_ge(mod_used, 2 * MOD_BATCH + PRIME_MOD)
            for s in ORDER:
                if s["name"] == "z":
                    sp.wait_ge(s_lzero, 1)
                    for d in range(2):
                        for g, name in enumerate(("lru_w_a", "lru_w_i")):
                            for b in range(2):
                                src = a[name][0, d].rearrange("(t b) j k -> b j t k", b=2)[b]
                                sp.dma_start(lru_w[64 * b:64 * b + 64, 2 * d + g, :, 64 * b:64 * b + 64], src).then_inc(s_lin, 16)
                if s["name"] == "up00":
                    sp.wait_ge(mod_t, MOD_ALL // MOD_BATCH)
                    sp.dma_start(cst[:, N_EARLY:], a["consts"][:, N_EARLY:]).then_inc(s_rope, 16)
                view = w_dram[s["w"]].rearrange("(h k p) c -> h p k c", p=P, k=UNIT_K)
                per_body = 2 * s["upp"]

                def load_body(it, js):
                    for j in js:
                        pair, part = j // s["upp"], j % s["upp"]
                        load_unit(view[s["kr"] // UNIT_K + part], it * per_body + (s["unit"] + j), j % RAW,
                                  it * (2 * UNIT_C) + (s["c0"] + pair * UNIT_C))

                peeled = 0
                if s["name"] == "out":
                    load_body(0, (0, 1))
                    sp.wait_ge(split_done, s["unit"] + 2 + PRIME_SPLIT)
                    load_mod(0, MOD_BATCH, (MOD_ALL // 2 - MOD_BATCH) // 2)
                    load_mod(1, MOD_ALL // 2, MOD_ALL // 4)
                    sp.wait_ge(mod_used, 2 * MOD_ALL + PRIME_MOD)
                    load_body(0, range(2, per_body))
                    peeled = 1
                with nc.Fori(peeled, s["bodies"], engines=[ENG.SP]) as it:
                    load_body(it, range(per_body))
            for n in range(2):
                sp.wait_ge(a_y, 2 * (n + 1))
                sp.dma_start(out[0, n * P:(n + 1) * P, :], o_tok[:, n]).then_inc(s_out, 16)
            sp.wait_ge(s_out, 32)

        @block.gpsimd
        def _(pool):
            nc.gpsimd.memset(lru_w[:, :, :, :], 0.0).then_inc(s_lzero, 1)
            nc.gpsimd.memset(cs[:, :, 2:], 0.0).then_inc(s_cs, 1)

        @block.scalar
        def _(act):
            def split_hi(u, j):
                act.wait_ge(raw_in[j % RAW], u_count(u, j))
                act.wait_ge(slot_free, u + 1)
                act.activation(w_hi[:, j % SPLIT], raw[:, j % RAW], ACT.Copy).then_inc(hi_ready, 1)

            def u_count(u, j):
                return (u - (j % RAW)) * (16 // RAW) + 16

            def mod_copy(b):
                act.wait_ge(mod_used, 2 * MOD_BATCH * (b + 1) + PRIME_MOD)
                act.activation(mod_row[:, :], bank[MODB][:, :], ACT.Copy).then_inc(mod_rows, 1)

            def alink(ins):
                acount[0] += 1
                ins.then_inc(link_a, 1)
                act.wait_ge(link_a, acount[0])

            def wait_alone(sem_, value):
                act.wait_ge(sem_, value)
                act.sem_inc(act_waits, 1)

            def tile_ps(pair, t, n=T):
                return bank[2 * pair + t][:, 0:n]

            def dyn(buf, i):
                return buf[:, bass.ds(i, 1)].rearrange("p a c -> p (a c)")

            def dynv(name, i):
                return vec[:, bass.ds(i + VEC[name], 1)]

            def segment(s, last=False):
                per_body = 2 * s["upp"]
                name = s["name"]

                def evac(it, pair):
                    if name[:2] in ("ou", "wo", "do"):
                        return
                    wait_alone(slot_free, it * per_body + (s["unit"] + (pair + 1) * s["upp"] + PRIME_SLOT))
                    for t in range(2):
                        tl = it * 4 + (2 * pair + t)
                        ps = tile_ps(pair, t)
                        if name == "xr":
                            act.activation(dyn(xc, tl), ps, ACT.Identity, bias=dynv("conv_b", tl),
                                           scale=dynv("conv_w", tl + 16)).then_inc(tap, 1)
                        if name == "qkv":
                            act.activation(dyn(qkv, tl), ps, ACT.Copy, scale=dynv("dn_conv", tl + 48)).then_inc(tap, 1)
                        if name == "z":
                            act.activation(dyn(siluz, tl), ps, ACT.Silu).then_inc(act_evac, 1)
                        if name == "yr":
                            act.activation(dyn(gy, tl), ps, ACT.Gelu_apprx_tanh).then_inc(act_evac, 1)
                        if name.startswith("up"):
                            n0 = 0 if "0" == name[2] else CTX
                            act.wait_ge(hid_done, it * 4 + (s["up"] + 2 * pair + t + 1))
                            act.activation(relu[:, 2 * pair + t, n0:T], tile_ps(pair, t, T - n0), ACT.Relu).then_inc(s_relu, 1)
                        if name == "q":
                            act.activation(dyn(q1, tl), tile_ps(pair, t, T - CTX), ACT.Copy).then_inc(act_evac, 1)
                        if name in "kv" and len(name) == 1:
                            act.activation(dyn(k1 if name == "k" else v1, tl), ps, ACT.Copy).then_inc(act_evac, 1)

                def after(it, pair):
                    if name == "qkv":
                        for t in range(2):
                            wait_alone(evac_done, it * 4 + (2 * s["pair"] + 2 * pair + t + 1 + PRIME_EVAC))
                            d_ = dyn(qkv, it * 4 + (2 * pair + t))
                            act.activation(d_, d_, ACT.Silu).then_inc(s_silu, 1)
                    if name.startswith("up"):
                        n0 = 0 if "0" == name[2] else CTX
                        for t in range(2):
                            wait_alone(s_sq, it * 4 + (s["up"] + 2 * pair + t + 1))
                            act.activation(bass_tok(hid_hi, it * 4 + (2 * pair + t), n0), relu[:, 2 * pair + t, n0:T],
                                           ACT.Copy).then_inc(s_hid, 1)

                def body(it, ahead):
                    u = s["unit"]
                    for j in range(2, s["upp"] + 2):
                        split_hi(it * per_body + (u + j), j)
                    evac(it, 0)
                    if name.startswith("up"):
                        after(it, 0)
                    for j in range(s["upp"] + 2, per_body + 2):
                        if j < per_body or ahead:
                            split_hi(it * per_body + (u + j), j)
                    if name == "qkv":
                        after(it, 0)
                    evac(it, 1)
                    after(it, 1)

                n = s["bodies"] - (1 if last else 0)
                with nc.Fori(0, n, engines=[ENG.Activation]) as it:
                    body(it, True)
                if last:
                    body(n, False)

            def bass_tok(buf, i, n0):
                return buf[:, bass.ds(i, 1), n0:T].rearrange("p a c -> p (a c)")

            def norm(sems_, layer, which, c0, before=None):
                n = T - c0
                segs = [x for x in SEGS if x[1] >= c0]
                for k in range(KT):
                    if before:
                        act.wait_ge(evac_done, 2 * SEG[before]["pair"] + k + 1 + PRIME_EVAC)
                    act.activation(n_sq[:, k, 0:n], xT[:, k, c0:T], ACT.Square).then_inc(sems_["sq"], 1)
                act.preload_act_table_set("natural_log_exp_and_others")
                act.wait_ge(sems_["ss"], KT)
                alink(act.activation(n_rt[:, 0:n], bank[X0][:, 0:n], ACT.Ln, scale=1.0 / D, bias=C("eps")))
                act.activation(n_rs[:, 0:n], n_rt[:, 0:n], ACT.Exp, scale=-0.5).then_inc(sems_["rt"], 1)
                if which is None:
                    return
                if before is None:
                    mod_copy(0)
                    split_hi(0, 0)
                    split_hi(1, 1)
                for k in range(KT):
                    act.wait_ge(sems_["t"], k + 1)
                    for v, t0, t1 in segs:
                        sh = modv[:, layer, 3 * which, k, v:v + 1]
                        act.activation(h_hi[:, k, t0:t1], n_t[:, k % 4, t0 - c0:t1 - c0], ACT.Identity, bias=sh)\
                           .then_inc(sems_["hi"], 1)

            act.wait_ge(s_vec, 1)
            act.activation(cs[:, :, 0:2].rearrange("p k v -> p v k"), V("c_ctx", 0, 16).rearrange("p (v k) -> p v k", v=2),
                           ACT.Silu).then_inc(s_cs, 1)
            for k in range(0, KT, 2):
                act.wait_ge(s_xps, k + 1)
                act.activation(xT[:, k], bank[X1][:, :], ACT.Copy).then_inc(s_xa, 1)
            act.wait_ge(s_xa, 4)
            act.wait_ge(s_xd, 4)
            norm(norm_sems["mix0"], 0, 0, 0)
            act.wait_ge(s_x, 48)
            act.activation(wg_hi[:, :, :], wg[:, :, :], ACT.Copy).then_inc(s_gate, 1)
            segment(SEG["xr"])
            segment(SEG["qkv"])
            act.wait_ge(s_gps, 1)
            gp = bank[X1][:, 0:NT * 32].rearrange("p (n c) -> p n c", c=32)
            act.activation(gate_raw[:, :, :], gp, ACT.Copy).then_inc(s_gate, 1)
            act.wait_ge(s_gate, 3)
            act.activation(beta[:, :, :], gate_raw[:, :, 0:16], ACT.Sigmoid)
            segment(SEG["z"])
            act.wait_ge(s_gate, 4)
            act.activation(sp_b[:, :], sp_a[:, :], ACT.Exp, scale=-1.0)
            act.activation(gate_bias[:, 1, :], gate_bias[:, 1, :], ACT.Exp).then_inc(s_gate, 1)
            segment(SEG["yr"])
            act.wait_ge(s_gps, 2)
            act.activation(neg_eg[:, :, :], bank[X1][:, 0:64].rearrange("p (n c) -> p n c", c=16), ACT.Exp)
            act.activation(e_rest[:, :, :], bank[X1][:, 64:128].rearrange("p (n c) -> p n c", c=16), ACT.Exp).then_inc(s_gate, 1)

            for b in range(4):
                for tt in range(2):
                    t_ = 2 * b + tt
                    act.wait_ge(s_lps, t_ + 1)
                    if t_ == 4:
                        mod_copy(1)
                    for d in range(2):
                        for g, (buf, bn) in enumerate(((l_a, "b_a"), (l_i, "b_i"))):
                            if b >= 1:
                                act.wait_ge(l_out, 2 * b)
                            act.activation(buf[:, 2 * d + tt], bank[2 * d + g][:, :], ACT.Sigmoid,
                                           bias=V(bn, 8 * d + t_)).then_inc(l_sig, 1)
                act.wait_ge(l_sig, 8 * (b + 1))
                for d in range(2):
                    for tt in range(2):
                        j, cc = 2 * d + tt, lru_c[:, 8 * d + 2 * b + tt:8 * d + 2 * b + tt + 1]
                        act.activation(l_t[:, j], l_a[:, j], ACT.Tanh, scale=cc).then_inc(link_a, 1)
                        acount[0] += 1
                        act.wait_ge(link_a, acount[0])
                        act.activation(l_a[:, j], l_a[:, j], ACT.Exp, scale=cc).then_inc(l_exp, 1)
                act.wait_ge(l_w, b + 1)
                act.activation(l_t[:, :, :], l_t[:, :, :], ACT.Sqrt, scale=-1.0).then_inc(l_sqrt, 1)

            def rstd(sems_, tiles, scale):
                act.preload_act_table_set("natural_log_exp_and_others")
                for i in range(len(tiles) + 1):
                    if i < len(tiles):
                        if i >= 2:
                            act.wait_ge(sems_["ss"], i - 1)
                        x_, n = tiles[i]
                        act.activation(sq2[:, i % 2, 0:n], x_, ACT.Square).then_inc(sems_["sq"], 1)
                    if i >= 1:
                        j = i - 1
                        n = tiles[j][1]
                        act.wait_ge(sems_["ss"], j + 1)
                        if j >= 2:
                            act.wait_ge(sems_["out"], j - 1)
                        alink(act.activation(rt2[:, j % 2, 0:n], bank[(X0, X1)[j % 2]][:, 0:n], ACT.Ln, scale=scale, bias=C("eps")))
                        act.activation(rs2[:, j % 2, 0:n], rt2[:, j % 2, 0:n], ACT.Exp, scale=-0.5).then_inc(sems_["rs"], 1)

            act.wait_ge(l_out, 8)
            act.wait_ge(evac_done, 2 * SEG["out"]["pair"] + PRIME_EVAC)
            act.wait_ge(s_silu, 24)
            rstd(l2, [(qkv[:, t_], T) for t_ in range(16)], 1.0)
            mod_copy(2)
            for ss, (hg, st, chunk) in enumerate(STEPS):
                if ss in MOD_TURN:
                    mod_copy(MOD_TURN[ss])
                seg_ = st // 2
                if st % 2 == 0:
                    for i in range(4):
                        n = i // 2
                        act.wait_ge(p_tok, (ss // 2) * 4 + i + 1)
                        dst = (k_tok, v_tok)[i % 2][:, n].rearrange("p a c -> p (a c)")
                        act.activation(dst, bank[(X2, X0)[i % 2]][:, :], ACT.Copy).then_inc(a_tok, 1)
                for g in range(2):
                    q_ = 2 * ss + g
                    act.wait_ge(p_dt, q_ + 1)
                    if ss >= 1:
                        act.wait_ge(v_s, q_ - 1)
                    act.activation(d_dt[:, g].rearrange("p a c -> p (a c)"), bank[BA[g]][:, :], ACT.Exp)
                    act.activation(d_eg[:, g].rearrange("p a c -> p (a c)"), bank[BB[g]][:, :], ACT.Exp).then_inc(a_dt, 1)
                for g in range(2):
                    q_ = 2 * ss + g
                    act.wait_ge(p_x1, q_ + 1)
                    act.activation(d_t[:, g].rearrange("p a c -> p (a c)"), bank[BB[g]][:, :], ACT.Copy).then_inc(a_t1, 1)
                for l in range(len(LEVELS)):
                    for g in range(2):
                        act.wait_ge(p_x, lev(ss, l, g))
                        act.activation(d_tt[:, g].rearrange("p a c -> p (a c)"), bank[BB[g]][:, :], ACT.Copy).then_inc(a_tt, 1)
                if st % 2 == 0:
                    for g in range(2):
                        act.wait_ge(p_o, 2 * ss + g + 1)
                        n = chunk[g]
                        act.activation(qkv[:, 16 + 4 * hg:20 + 4 * hg, n * P:(n + 1) * P],
                                       bank[BB[g]][:, :].rearrange("p (a c) -> p a c", a=4), ACT.Copy).then_inc(a_o, 1)
            mod_copy(5)
            act.wait_ge(v_o, 8)
            act.wait_ge(v_s, 16)
            for t_ in range(16):
                if t_ == 8:
                    rstd(dnn, [(qkv[:, 16 + h], T) for h in range(8)], 1.0 / P)
                if t_ >= 8:
                    act.wait_ge(dnn["out"], t_ - 8 + 1)
                act.activation(mix_hi[:, t_], xc[:, t_] if t_ < 8 else qkv[:, 8 + t_], ACT.Copy).then_inc(s_mix_hi, 1)
            segment(SEG["out"])

            def mlp(layer, last):
                nm = f"mlp{layer}"
                norm(norm_sems[nm], layer, 1, 0 if layer == 0 else CTX, ("out", "wo")[layer])
                for half in (0, 1):
                    segment(SEG[f"up{layer}{half}"])
                    segment(SEG[f"down{layer}{half}"], last and half == 1)

            mlp(0, False)
            norm(norm_sems["mix1"], 1, 0, 0, "down01")
            for nm in ("q", "k", "v"):
                segment(SEG[nm])
            act.wait_ge(act_evac, 32)
            rstd(qkn, [(q1[:, h], T - CTX) for h in range(8)] + [(k1[:, h], T) for h in range(4)], 1.0 / P)
            for h in range(4):
                act.wait_ge(p_v1, h + 1)
                act.activation(v1_tok[:, h].rearrange("p a c -> p (a c)"), bank[(X2, 3)[h % 2]][:, :], ACT.Copy).then_inc(a_v1, 1)

            def heads_out(h):
                act.wait_ge(p_pv, 2 * h + 2)
                act.activation(att_hi[:, h, CTX:T], bank[(X0, X1)[h % 2]][:, 0:T - CTX], ACT.Copy).then_inc(a_ah, 1)

            for i in range(17):
                if i < 16:
                    act.wait_ge(v_mx, i + 1)
                    if i >= 2:
                        act.wait_ge(p_pt, i - 1)
                    act.activation(prob[:, i % 2], bank[i % 2][:, :], ACT.Exp, scale=float(P) ** -0.5,
                                   bias=smx[:, 1, i:i + 1], accum_out=smx[:, 2, i:i + 1]).then_inc(a_ex, 1)
                if i >= 1:
                    j = i - 1
                    act.wait_ge(p_pt, j + 1)
                    if j >= 2:
                        act.wait_ge(p_pv, j - 1)
                    act.activation(probT[:, j % 2].rearrange("p a c -> p (a c)"), bank[2 + j % 2][:, :], ACT.Copy).then_inc(a_pt, 1)
                if i >= 4 and i % 2 == 0:
                    heads_out(i // 2 - 2)
            heads_out(7)
            segment(SEG["wo"])
            mlp(1, True)
            norm(norm_sems["fin"], 1, None, CTX, "down11")
            for i in range(4):
                act.wait_ge(p_y, i + 1)
                act.activation(o_tok[:, i // 2, (i % 2) * 512:(i % 2) * 512 + 512], bank[i][:, :], ACT.Copy).then_inc(a_y, 1)

        @block.vector
        def _(dve):
            dve.sem_inc(split_done, PRIME_SPLIT)
            dve.sem_inc(evac_done, PRIME_EVAC)
            dve.sem_inc(hid_done, PRIME_HID)

            def link(ins):
                dcount[0] += 1
                ins.then_inc(link_d, 1)
                dve.wait_ge(link_d, dcount[0])

            def split_lo(u, j):
                dve.wait_ge(hi_ready, u + 1)
                dve.tensor_tensor(w_lo[:, j % SPLIT], raw[:, j % RAW], w_hi[:, j % SPLIT].bitcast(F32),
                                  ALU.subtract).then_inc(split_done, 1)

            def dyn(buf, i, t0=0, t1=T):
                return buf[:, bass.ds(i, 1), t0:t1].rearrange("p a c -> p (a c)")

            def dyn2(buf, i):
                return buf[:, bass.ds(i, 1)].rearrange("p a (s c) -> p (a s) c", s=2)

            def segment(s, last=False):
                per_body = 2 * s["upp"]
                name = s["name"]

                def evac(it, pair):
                    ps_done = it * per_body + (s["unit"] + (pair + 1) * s["upp"] + PRIME_SLOT)
                    if name in ("xr", "qkv"):
                        buf, cn, nt_, base_, cb = (xc, "conv_w", 8, 0, 0) if name == "xr" else (qkv, "dn_conv", 24, 8, 24)
                        cb = 2 * s["pair"]
                        for n, (j, o0, i0, w_) in enumerate(((1, 1, 0, 255), (0, 2, 0, 254), (3, 0, 1, 255))):
                            for t in range(2):
                                tl = it * 4 + (2 * pair + t)
                                if n == 0:
                                    dve.wait_ge(tap, tl + (2 * s["pair"] + 1))
                                else:
                                    dve.wait_ge(conv_step, it * 8 + (4 * s["pair"] + 4 * pair + 2 * (n - 1) + t + 1))
                                y = dyn2(buf, tl)
                                x_ = bank[2 * pair + t][:, :].rearrange("p (s c) -> p s c", s=2)
                                ins = dve.scalar_tensor_tensor(
                                    out=y[:, :, o0:o0 + w_], in0=x_[:, :, i0:i0 + w_],
                                    scalar=vec[:, bass.ds(tl + (VEC[cn] + j * nt_), 1)], in1=y[:, :, o0:o0 + w_],
                                    op0=ALU.mult, op1=ALU.add)
                                ins.then_inc(conv_step if n < 2 else evac_done, 1)
                    elif name in ("z", "yr", "q", "k", "v"):
                        for t in range(2):
                            dve.wait_ge(act_evac, it * 4 + (2 * (s["pair"] - act_base(name)) + 2 * pair + t + 1))
                            dve.sem_inc(evac_done, 1)
                    elif name.startswith("up"):
                        n0 = 0 if "0" == name[2] else CTX
                        for t in range(2):
                            dve.wait_ge(s_relu, it * 4 + (s["up"] + 2 * pair + t + 1))
                            r_ = relu[:, 2 * pair + t, n0:T]
                            dve.tensor_tensor(r_, r_, r_, ALU.mult).then_inc(s_sq, 1)
                            dve.sem_inc(evac_done, 1)
                        for t in range(2):
                            dve.wait_ge(s_hid, it * 4 + (s["up"] + 2 * pair + t + 1))
                            tl = it * 4 + (2 * pair + t)
                            dve.tensor_tensor(dyn(hid_lo, tl, n0), relu[:, 2 * pair + t, n0:T],
                                              dyn(hid_hi, tl, n0).bitcast(F32), ALU.subtract).then_inc(hid_done, 1)
                    else:
                        layer, part = (0, 2) if name == "out" else (1, 2) if name == "wo" else (int(name[4]), 5)
                        c0 = 0 if layer == 0 else CTX
                        dve.wait_ge(slot_free, ps_done)
                        for t in range(2):
                            tl = it * 4 + (2 * pair + t)
                            for v, t0, t1 in SEGS:
                                if t0 < c0:
                                    continue
                                y = dyn(xT, tl, t0, t1)
                                ins = dve.scalar_tensor_tensor(
                                    out=y, in0=bank[2 * pair + t][:, t0 - c0:t1 - c0],
                                    scalar=modv[:, layer, part, bass.ds(tl, 1), v:v + 1].rearrange("p a c -> p (a c)"),
                                    in1=y, op0=ALU.mult, op1=ALU.add)
                            ins.then_inc(evac_done, 1)

                def body(it, ahead):
                    u = s["unit"]
                    for j in range(2, s["upp"] + 2):
                        split_lo(it * per_body + (u + j), j)
                    evac(it, 0)
                    for j in range(s["upp"] + 2, per_body + 2):
                        if j < per_body or ahead:
                            split_lo(it * per_body + (u + j), j)
                    evac(it, 1)

                n = s["bodies"] - (1 if last else 0)
                with nc.Fori(0, n, engines=[ENG.DVE]) as it:
                    body(it, True)
                if last:
                    body(n, False)

            def act_base(name):
                return {"z": SEG["z"]["pair"], "yr": SEG["z"]["pair"]}.get(name, SEG["q"]["pair"] - 8)

            def evac_mod(b):
                dve.wait_ge(mod_t, b + 1)
                for half in range(2):
                    t_ = 16 * b + 8 * half
                    ps = bank[MODB][:, 256 * half:256 * half + 256].rearrange("p (i g w) -> p g i w", i=2, g=4)[:, :, :, 0:2]
                    b_ = V("b_mod", t_, 8).rearrange("p (g i) -> p g i", i=2).unsqueeze(3).to_broadcast([P, 4, 2, 2])
                    o_ = modv[:, :, :, :, :].rearrange("p l a k v -> p (l a k) v")[:, t_:t_ + 8]
                    link(dve.tensor_tensor(o_.rearrange("p (g i) v -> p g i v", i=2), ps, b_, ALU.add))
                dve.sem_inc(s_mod, 1)

            def make_gain(layer, which):
                g_ = V("mix_g" if which == 0 else "mlp_g", 8 * layer, 8).unsqueeze(2).to_broadcast([P, 8, 2])
                link(dve.scalar_tensor_tensor(out=gain[:, layer, which], in0=modv[:, layer, 3 * which + 1], scalar=1.0,
                                              in1=g_, op0=ALU.add, op1=ALU.mult))

            def norm(sems_, layer, which, c0):
                n = T - c0
                segs = [x for x in SEGS if x[1] >= c0]
                dve.wait_ge(sems_["rt"], 1)
                if which is None:
                    return

                def scaled(k):
                    if k >= 4:
                        dve.wait_ge(sems_["lo"], k - 3)
                    for i, (v, t0, t1) in enumerate(segs):
                        ins = dve.scalar_tensor_tensor(out=n_t[:, k % 4, t0 - c0:t1 - c0], in0=xT[:, k, t0:t1],
                                                       scalar=gain[:, layer, which, k, v:v + 1],
                                                       in1=n_rs[:, t0 - c0:t1 - c0], op0=ALU.mult, op1=ALU.mult)
                    ins.then_inc(sems_["t"], 1)

                def low(k):
                    dve.wait_ge(sems_["hi"], len(segs) * (k + 1))
                    for v, t0, t1 in segs:
                        ins = dve.scalar_tensor_tensor(out=h_lo[:, k, t0:t1], in0=n_t[:, k % 4, t0 - c0:t1 - c0],
                                                       scalar=modv[:, layer, 3 * which, k, v:v + 1],
                                                       in1=h_hi[:, k, t0:t1].bitcast(F32), op0=ALU.add, op1=ALU.subtract)
                    ins.then_inc(sems_["lo"], 1)

                scaled(0)
                scaled(1)
                for k in range(KT):
                    if k + 2 < KT:
                        scaled(k + 2)
                    low(k)

            dve.wait_ge(s_rows, 1)
            dve.tensor_copy(vec[:, 0:P], bank[X0][:, 0:P])
            dve.tensor_copy(vec[:, VEC_B:VEC_B + VEC_B_ROWS], bank[X0][:, P:P + VEC_B_ROWS])
            dve.tensor_copy(vec[:, VEC_C:VEC_C + 96], bank[X0][:, 2 * P:2 * P + 96]).then_inc(s_vec, 1)
            for k in range(1, KT, 2):
                dve.wait_ge(s_xps, k + 1)
                dve.tensor_copy(xT[:, k], bank[X2][:, :]).then_inc(s_xd, 1)
            dve.wait_ge(s_vec, 1)
            evac_mod(0)
            make_gain(0, 0)
            split_lo(0, 0)
            split_lo(1, 1)
            norm(norm_sems["mix0"], 0, 0, 0)

            dve.wait_ge(s_gate, 1)
            dve.tensor_tensor(wg_lo[:, :, :], wg[:, :, :], wg_hi[:, :, :].bitcast(F32), ALU.subtract).then_inc(s_gate, 1)
            segment(SEG["xr"])
            segment(SEG["qkv"])
            dve.wait_ge(s_gate, 3)
            link(dve.tensor_tensor(sp_x[:, 0:64].rearrange("p (n c) -> p n c", c=16), gate_raw[:, :, 16:32],
                                   gate_bias[:, 0, :].unsqueeze(1).to_broadcast([P, NT, 16]), ALU.add))
            link(dve.tensor_scalar(sp_x[:, 64:80], V("lam", 0, 16), -1.0, None, ALU.mult))
            dve.scalar_tensor_tensor(out=sp_a[:, :], in0=sp_x[:, :], scalar=-1.0, in1=sp_x[:, :], op0=ALU.mult,
                                     op1=ALU.max).then_inc(s_gate, 1)
            segment(SEG["z"])
            dve.wait_ge(s_gate, 5)
            link(dve.tensor_scalar(sp_a[:, :], sp_b[:, :], 2.0, None, ALU.add))
            link(dve.reciprocal(sp_a[:, :], sp_a[:, :]))
            link(dve.tensor_tensor(sp_a[:, :], sp_a[:, :], sp_b[:, :], ALU.mult))
            link(dve.tensor_tensor(sp_b[:, :], sp_a[:, :], sp_a[:, :], ALU.mult))
            link(dve.tensor_scalar(sp_p[:, :], sp_b[:, :], 1.0 / 17, None, ALU.mult))
            for n in range(15, 1, -2):
                link(dve.scalar_tensor_tensor(out=sp_p[:, :], in0=sp_p[:, :], scalar=1.0 / n, in1=sp_b[:, :], op0=ALU.add,
                                              op1=ALU.mult))
            link(dve.scalar_tensor_tensor(out=sp_p[:, :], in0=sp_p[:, :], scalar=1.0, in1=sp_a[:, :], op0=ALU.add, op1=ALU.mult))
            link(dve.tensor_scalar(sp_x[:, :], sp_x[:, :], 0.0, None, ALU.max))
            link(dve.scalar_tensor_tensor(out=sp_x[:, :], in0=sp_p[:, :], scalar=2.0, in1=sp_x[:, :], op0=ALU.mult, op1=ALU.add))
            link(dve.scalar_tensor_tensor(out=g_log[:, :, :], in0=sp_x[:, 0:64].rearrange("p (n c) -> p n c", c=16), scalar=-1.0,
                                          in1=gate_bias[:, 1, :].unsqueeze(1).to_broadcast([P, NT, 16]), op0=ALU.mult,
                                          op1=ALU.mult))
            dve.tensor_scalar(lru_c, lru_c, -LRU_C, None, ALU.mult).then_inc(s_gate, 1)
            segment(SEG["yr"])

            for b in range(4):
                dve.wait_ge(l_exp, 4 * (b + 1))
                link(dve.tensor_tensor(l_q[:, :, :], l_a[:, :, :], l_a[:, :, :], ALU.mult))
                dve.scalar_tensor_tensor(out=l_t[:, :, :], in0=l_q[:, :, :], scalar=1.0, in1=l_t[:, :, :], op0=ALU.add,
                                         op1=ALU.mult).then_inc(l_w, 1)
                for d in range(2):
                    ins = dve.tensor_tensor(l_i[:, 2 * d:2 * d + 2], l_i[:, 2 * d:2 * d + 2], xc[:, 2 * b:2 * b + 2], ALU.mult)
                link(ins)
                dve.wait_ge(l_sqrt, b + 1)
                link(dve.tensor_tensor(l_i[:, :, :], l_i[:, :, :], l_t[:, :, :], ALU.mult))
                for tt in range(2):
                    dve.tensor_tensor_scan(l_q[:, tt], l_a[:, tt], l_i[:, tt], 0.0, ALU.mult, ALU.add)
                    j = 2 + tt
                    ins = dve.tensor_tensor_scan(l_q[:, j, CTX - 1::-1], l_a[:, j, CTX - 1::-1], l_i[:, j, CTX - 1::-1],
                                                 0.0, ALU.mult, ALU.add)
                link(ins)
                for tt in range(2):
                    j = 2 + tt
                    ins = dve.tensor_tensor_scan(l_q[:, j, T - 1:CTX - 1:-1], l_a[:, j, T - 1:CTX - 1:-1],
                                                 l_i[:, j, T - 1:CTX - 1:-1], l_q[:, j, 0:1], ALU.mult, ALU.add)
                link(ins)
                link(dve.tensor_tensor(l_q[:, 0:2], l_q[:, 0:2], l_q[:, 2:4], ALU.add))
                dve.tensor_tensor(xc[:, 2 * b:2 * b + 2], l_q[:, 0:2], gy[:, 2 * b:2 * b + 2], ALU.mult).then_inc(l_out, 2)
                if b == 2:
                    evac_mod(1)

            dve.wait_ge(s_gate, 7)
            link(dve.tensor_scalar(neg_eg[:, :, :], neg_eg[:, :, :], -1.0, None, ALU.mult))
            for t_ in range(16):
                dve.wait_ge(l2["rs"], t_ + 1)
                dve.scalar_tensor_tensor(out=qkv[:, t_], in0=qkv[:, t_], scalar=float(P) ** -0.5 if t_ < 8 else 1.0,
                                         in1=rs2[:, t_ % 2], op0=ALU.mult, op1=ALU.mult).then_inc(l2["out"], 1)
            evac_mod(2)
            for ss, (hg, st, chunk) in enumerate(STEPS):
                heads = slice(4 * hg, 4 * hg + 4)

                def cols(buf, g):
                    n = chunk[g]
                    return buf[:, n, 8 * g + 4 * hg:8 * g + 4 * hg + 4].unsqueeze(2).to_broadcast([P, 4, P])

                def mask(name, w_=P):
                    return C(name).unsqueeze(1).to_broadcast([P, 4, w_])

                def flat(ap):
                    return ap.rearrange("p a c -> p (a c)")

                def ps4(b_, c0_=0, w_=P):
                    return bank[b_][:, c0_:c0_ + 4 * w_].rearrange("p (a c) -> p a c", a=4)

                if st == 0:
                    if ss:
                        dve.wait_ge(p_s, 2 * ss)
                    link(dve.memset(d_s[:, :, :, :], 0.0))
                    if ss == 0:
                        dve.wait_ge(l2["out"], 16)
                        dve.sem_inc(v_s0, 1)
                for g in range(2):
                    if ss:
                        dve.wait_ge(p_s, 2 * ss - 1 + g)
                    dve.tensor_tensor(d_gu[:, g], mask(("le", "ge")[g]), cols(g_log, g), ALU.mult).then_inc(v_gu, 1)
                for g in range(2):
                    q_ = 2 * ss + g
                    dve.wait_ge(a_dt, q_ + 1)
                    dve.wait_ge(p_kk, 2 * q_ + 1)
                    for a_ in range(4):
                        ins = dve.scalar_tensor_tensor(out=d_n[:, g, a_], in0=bank[BC[g]][:, a_ * P:(a_ + 1) * P],
                                                       scalar=beta[:, chunk[g], 8 * g + 4 * hg + a_:8 * g + 4 * hg + a_ + 1],
                                                       in1=d_dt[:, g, a_], op0=ALU.mult, op1=ALU.mult)
                    ins.then_inc(v_n, 1)
                    dve.wait_ge(v_n, q_ + 1)
                    link(dve.tensor_tensor(d_r[:, g], d_n[:, g], mask(("pair_f", "pair_r")[g]), ALU.mult))
                    dve.tensor_tensor(d_tt[:, g], mask("ident"), d_r[:, g], ALU.subtract).then_inc(v_tt, 1)
                for g in range(2):
                    q_ = 2 * ss + g
                    n = chunk[g]
                    dve.wait_ge(p_kk, 2 * q_ + 2)
                    link(dve.tensor_tensor(d_at[:, g], ps4(BA[g]), d_dt[:, g], ALU.mult))
                    dve.tensor_tensor(d_qd[:, g], qkv[:, heads, n * P:(n + 1) * P], d_eg[:, g], ALU.mult)
                    dve.tensor_tensor(d_at[:, g], d_at[:, g], mask(("le", "ge")[g]), ALU.mult).then_inc(v_at, 1)
                for l, s_ in enumerate(LEVELS):
                    for g in range(2):
                        dve.wait_ge(p_p, lev(ss, l, g))
                        dve.tensor_tensor(d_pc[:, g], ps4(BA[g], 0, P // 2), mask(f"m{s_}_" + "fr"[g], P // 2), ALU.mult)\
                           .then_inc(v_pc, 1)
                    if l == 0:
                        for g in range(2):
                            dve.wait_ge(p_ks, 2 * ss + g + 1)
                            dve.wait_ge(a_tok, 4 * (ss // 2 + 1))
                            for a_ in range(4):
                                c_ = 8 * g + 4 * hg + a_
                                ins = dve.scalar_tensor_tensor(out=d_r[:, g, a_], in0=bank[BC[g]][:, a_ * P:(a_ + 1) * P],
                                                               scalar=neg_eg[:, chunk[g], c_:c_ + 1], in1=v_tok[:, chunk[g] % 2, a_],
                                                               op0=ALU.mult, op1=ALU.add)
                            ins.then_inc(v_r, 1)
                    for g in range(2):
                        dve.wait_ge(p_tp, lev(ss, l, g))
                        y_ = half_cols(d_t, g, None, s_)
                        x_ = bank[BA[g]][:, 256:512].rearrange("p (b s) -> p b s", s=s_)
                        dve.tensor_tensor(y_, y_, x_, ALU.subtract).then_inc(v_t, 1)
                if ss in MOD_TURN:
                    evac_mod(MOD_TURN[ss])
                for g in range(2):
                    dve.wait_ge(p_vn, 2 * ss + g + 1)
                    dve.tensor_tensor(d_vn[:, g], ps4(BA[g]), cols(beta, g), ALU.mult).then_inc(v_vn, 1)
                    dve.wait_ge(v_vn, 2 * ss + g + 1)
                    dve.tensor_tensor(d_vd[:, g], d_vn[:, g], cols(e_rest, g), ALU.mult).then_inc(v_vd, 1)
                for g in range(2):
                    dve.wait_ge(p_s, 2 * ss + g + 1)
                    last_col = (P - 1, 0)[g]
                    for a_ in range(4):
                        ins = dve.scalar_tensor_tensor(out=d_s[:, g, a_], in0=d_s[:, g, a_],
                                                       scalar=d_eg[:, g, a_, last_col:last_col + 1],
                                                       in1=bank[BC[g]][:, a_ * P:(a_ + 1) * P], op0=ALU.mult, op1=ALU.add)
                    ins.then_inc(v_s, 1)
                    dve.wait_ge(v_s, 2 * ss + g + 1)
                if st % 2 == 1:
                    for g in range(2):
                        n = chunk[g]
                        y_ = qkv[:, 16 + 4 * hg:20 + 4 * hg, n * P:(n + 1) * P]
                        dve.wait_ge(a_o, 2 * (ss // 2) + 2)
                        dve.tensor_tensor(y_, y_, ps4(BB[g]), ALU.add).then_inc(v_o, 1)
            evac_mod(5)
            make_gain(0, 1)
            make_gain(1, 0)
            make_gain(1, 1)
            for t_ in range(8):
                dve.wait_ge(s_mix_hi, t_ + 1)
                dve.tensor_tensor(mix_lo[:, t_], xc[:, t_], mix_hi[:, t_].bitcast(F32), ALU.subtract).then_inc(s_mix_lo, 1)
            for h in range(8):
                dve.wait_ge(dnn["rs"], h + 1)
                y_ = qkv[:, 16 + h]
                link(dve.scalar_tensor_tensor(out=y_, in0=y_, scalar=V("dn_g"), in1=rs2[:, h % 2], op0=ALU.mult, op1=ALU.mult))
                dve.tensor_tensor(y_, y_, siluz[:, h], ALU.mult).then_inc(dnn["out"], 1)
            for h in range(8):
                dve.wait_ge(s_mix_hi, 9 + h)
                dve.tensor_tensor(mix_lo[:, 8 + h], qkv[:, 16 + h], mix_hi[:, 8 + h].bitcast(F32), ALU.subtract)\
                   .then_inc(s_mix_lo, 1)
            segment(SEG["out"])

            def mlp(layer, last):
                norm(norm_sems[f"mlp{layer}"], layer, 1, 0 if layer == 0 else CTX)
                for half in (0, 1):
                    segment(SEG[f"up{layer}{half}"])
                    segment(SEG[f"down{layer}{half}"], last and half == 1)

            mlp(0, False)
            norm(norm_sems["mix1"], 1, 0, 0)
            for nm in ("q", "k", "v"):
                segment(SEG[nm])
            for i in range(12):
                dve.wait_ge(qkn["rs"], i + 1)
                y_, n, gn = (q1[:, i], T - CTX, "q_g") if i < 8 else (k1[:, i - 8], T, "k_g")
                dve.scalar_tensor_tensor(out=y_, in0=y_, scalar=V(gn), in1=rs2[:, i % 2, 0:n], op0=ALU.mult, op1=ALU.mult)\
                   .then_inc(qkn["out"], 1)
            dve.wait_ge(s_rope, 16)
            for i in range(6):
                b_ = i % 2
                y_ = q1[:, 2 * i:2 * i + 2, :] if i < 4 else k1[:, 2 * i - 8:2 * i - 6, CTX:T]
                cos, sin = (C(x).unsqueeze(1).to_broadcast([P, 2, T - CTX]) for x in ("cos", "sin"))
                dve.tensor_tensor(rope_a[:, b_], y_, cos, ALU.mult)
                dve.wait_ge(p_rot, i + 1)
                link(dve.tensor_tensor(rope_b[:, b_], bank[b_][:, :].rearrange("p (a c) -> p a c", a=2), sin, ALU.mult))
                dve.tensor_tensor(y_, rope_a[:, b_], rope_b[:, b_], ALU.add).then_inc(v_rope, 1)

            def head_low(h):
                dve.wait_ge(a_ah, h + 1)
                dve.tensor_tensor(att_lo[:, h, CTX:T], bank[(X0, X1)[h % 2]][:, 0:T - CTX], att_hi[:, h, CTX:T].bitcast(F32),
                                  ALU.subtract).then_inc(v_al, 1)

            for i in range(17):
                if i < 16:
                    dve.wait_ge(p_sc, i + 1)
                    link(dve.tensor_reduce(smx[:, 0, i:i + 1], bank[i % 2][:, :], mybir.AxisListType.X, ALU.max))
                    dve.tensor_scalar(smx[:, 1, i:i + 1], smx[:, 0, i:i + 1], -float(P) ** -0.5, None, ALU.mult).then_inc(v_mx, 1)
                if i < 16:
                    dve.wait_ge(a_ex, i + 1)
                    link(dve.reciprocal(smx[:, 2, i:i + 1], smx[:, 2, i:i + 1]))
                    dve.tensor_scalar(prob[:, i % 2], prob[:, i % 2], smx[:, 2, i:i + 1], None, ALU.mult).then_inc(v_pr, 1)
                if i >= 4 and i % 2 == 0:
                    head_low(i // 2 - 2)
            head_low(7)
            segment(SEG["wo"])
            mlp(1, True)
            norm(norm_sems["fin"], 1, None, CTX)
            for k in range(KT):
                dve.scalar_tensor_tensor(out=y_out[:, k], in0=xT[:, k, CTX:T], scalar=V("final_g", k), in1=n_rs[:, 0:T - CTX],
                                         op0=ALU.mult, op1=ALU.mult).then_inc(v_y, 1)

        @block.tensor
        def _(pe):
            pe.sem_inc(slot_free, PRIME_SLOT)
            pe.sem_inc(mod_used, PRIME_MOD)

            def mod_unit(m, j, chunk_in_half, col):
                pe.wait_ge(mod_in[j % RAW], (m - (j % RAW)) * (16 // RAW) + 16)
                r0 = 32 * chunk_in_half
                for k in range(UNIT_K):
                    kk = (j % 2) * UNIT_K + k
                    mm = pe.matmul(bank[MODB][r0:r0 + 32, col:col + UNIT_C], cs[:, kk], raw[:, j % RAW, k],
                                   start=(kk == 0), stop=(kk == KT - 1), tile_position=(0, r0))
                mm.then_inc(mod_used, 1)

            def mod_flip(b):
                pe.wait_ge(mod_rows, b + 1)
                for i in range(4):
                    mm = pe.transpose(bank[MODB][:, i * P:(i + 1) * P], mod_row[:, i * P:(i + 1) * P], C("ident"))
                mm.then_inc(mod_t, 1)

            mod_next = [0]

            def mod_filler(n):
                for _ in range(n):
                    m = mod_next[0]
                    b, c = m // (2 * MOD_BATCH), m // 2 % MOD_BATCH
                    if b and m % (2 * MOD_BATCH) == 0:
                        pe.wait_ge(s_mod, b)
                    mod_unit(m, m % RAW, c % 4, c // 4 * UNIT_C)
                    mod_next[0] += 1

            def segment(s, hi, lo, n0, ready=None):
                per_body = 2 * s["upp"]
                kt = s["kt"]

                def body(it, first):
                    for j in range(per_body):
                        pair, part = j // s["upp"], j % s["upp"]
                        pe.wait_ge(split_done, it * per_body + (s["unit"] + j + 1 + PRIME_SPLIT))
                        if part == 0:
                            pe.wait_ge(evac_done, it * 4 + (2 * (s["pair"] + pair) + 2))
                        for k in range(UNIT_K):
                            kk = part * UNIT_K + k
                            if first and pair == 0:
                                ready(kk)
                            for t in range(2):
                                for n, (w, h) in enumerate(((w_hi, hi), (w_hi, lo), (w_lo, hi))):
                                    mm = pe.matmul(bank[2 * pair + t][:, 0:T - n0], w[:, j % SPLIT, k, t * P:(t + 1) * P],
                                                   h[:, kk, n0:T], start=(kk == 0 and n == 0), stop=(kk == kt - 1 and n == 2))
                        mm.then_inc(slot_free, 1)

                if ready:
                    body(0, True)
                with nc.Fori(1 if ready else 0, s["bodies"], engines=[ENG.PE]) as it:
                    body(it, False)

            def normed(name):
                return lambda k: pe.wait_ge(norm_sems[name]["lo"], k + 1)

            def sumsq(sems_, n):
                for k in range(KT):
                    pe.wait_ge(sems_["sq"], k + 1)
                    pe.matmul(bank[X0][:, 0:n], C("ones"), n_sq[:, k, 0:n], start=(k == 0), stop=(k == KT - 1))\
                      .then_inc(sems_["ss"], 1)

            pe.wait_ge(s_in, 18 * 16)
            pe.transpose(bank[X0][:, 0:P], rowsA[:, :], C("ident"))
            pe.transpose(bank[X0][:, P:P + VEC_B_ROWS], rowsB[0:VEC_B_ROWS, :], C("ident")[0:VEC_B_ROWS, 0:VEC_B_ROWS])
            pe.transpose(bank[X0][:, 2 * P:2 * P + 96], rowsC[0:96, :], C("ident")[0:96, 0:96]).then_inc(s_rows, 1)
            pe.wait_ge(s_x, 48)
            for k in range(KT):
                if k >= 2:
                    pe.wait_ge((s_xa, s_xd)[k % 2], k // 2)
                for n in range(NT):
                    mm = pe.transpose(bank[(X1, X2)[k % 2]][:, n * P:(n + 1) * P], xin[:, n, k * P:(k + 1) * P], C("ident"))
                mm.then_inc(s_xps, 1)
            pe.wait_ge(s_cs, 1)
            pe.wait_ge(s_xd, 4)
            sumsq(norm_sems["mix0"], T)
            pe.wait_ge(s_cs, 2)
            mod_filler(2 * MOD_BATCH)
            mod_flip(0)
            segment(SEG["xr"], h_hi, h_lo, 0, normed("mix0"))
            pe.wait_ge(s_gate, 2)
            for n in range(NT):
                for k in range(KT):
                    for i, (h, w) in enumerate(((h_hi, wg_hi), (h_hi, wg_lo), (h_lo, wg_hi))):
                        mm = pe.matmul(bank[X1][:, n * 32:n * 32 + 32], h[:, k, n * P:(n + 1) * P], w[:, k],
                                       start=(k == 0 and i == 0), stop=(k == KT - 1 and i == 2))
            mm.then_inc(s_gps, 1)
            for nm in ("qkv", "z", "yr"):
                segment(SEG[nm], h_hi, h_lo, 0)
            pe.wait_ge(s_gate, 6)
            for n in range(NT):
                for d in range(2):
                    rhs = g_log[:, n, 8 * d:8 * d + 8]
                    pe.matmul(bank[X1][:, n * 16 + 8 * d:n * 16 + 8 * d + 8], C(("le", "ge")[d]), rhs, start=True, stop=True)
                    mm = pe.matmul(bank[X1][:, 64 + n * 16 + 8 * d:64 + n * 16 + 8 * d + 8], C(("gt", "lt")[d]), rhs,
                                   start=True, stop=True)
            mm.then_inc(s_gps, 1)
            pe.wait_ge(s_lin, 8 * 16)
            pe.wait_ge(evac_done, 2 * SEG["out"]["pair"] + PRIME_EVAC)
            for t_ in range(8):
                if t_ >= 1:
                    pe.wait_ge(l_sig, 4 * t_)
                for d in range(2):
                    for g in range(2):
                        mm = pe.matmul(bank[2 * d + g][:, :], lru_w[:, 2 * d + g, t_], xc[:, t_], start=True, stop=True)
                mm.then_inc(s_lps, 1)
                if t_ == 4:
                    mod_flip(1)
                mod_filler((0, 7, 3, 6, 0, 0, 0, 16)[t_])
            def sums(sems_, widths):
                for i, n in enumerate(widths):
                    pe.wait_ge(sems_["sq"], i + 1)
                    if i >= 2:
                        pe.wait_ge(sems_["rs"], i - 1)
                    pe.matmul(bank[(X0, X1)[i % 2]][:, 0:n], C("ones"), sq2[:, i % 2, 0:n], start=True, stop=True)\
                      .then_inc(sems_["ss"], 1)

            pe.wait_ge(s_gate, 7)
            sums(l2, [T] * 16)
            pe.wait_ge(l2["rs"], 16)
            mod_flip(2)
            pe.wait_ge(v_s0, 1)
            for ss, (hg, st, chunk) in enumerate(STEPS):

                fill = (0,) * 5 if ss in MOD_TURN else (2, 2, 2, 1, 1)

                def feat(tile0, a_, g):
                    n = chunk[g]
                    return qkv[:, tile0 + 4 * hg + a_, n * P:(n + 1) * P]

                if st % 2 == 0:
                    for i in range(4):
                        n = st + i // 2
                        if i >= 2:
                            pe.wait_ge(a_tok, (ss // 2) * 4 + i - 1)
                        elif ss:
                            pe.wait_ge(v_s, 2 * ss)
                            pe.wait_ge(v_o, 2 * (ss // 2))
                        for a_ in range(4):
                            mm = pe.transpose(bank[(X2, X0)[i % 2]][:, a_ * P:(a_ + 1) * P],
                                              qkv[:, (8, 16)[i % 2] + 4 * hg + a_, n * P:(n + 1) * P], C("ident"))
                        mm.then_inc(p_tok, 1)
                for g in range(2):
                    pe.wait_ge(v_gu, 2 * ss + g + 1)
                    if ss:
                        pe.wait_ge(a_o, 2 * ((ss + 1) // 2))
                        if ss >= 2:
                            pe.wait_ge(v_o, 2 * (ss // 2))
                    gu = d_gu[:, g].rearrange("p a c -> p (a c)")
                    pe.matmul(bank[BA[g]][:, :], C(("gt", "lt")[g]), gu, start=True, stop=True)
                    pe.matmul(bank[BB[g]][:, :], C("ones"), gu, start=True, stop=True).then_inc(p_dt, 1)
                if ss in MOD_TURN:
                    mod_flip(MOD_TURN[ss])
                mod_filler(fill[0])
                for g in range(2):
                    q_ = 2 * ss + g
                    if st % 2 == 0:
                        pe.wait_ge(a_tok, 4 * (ss // 2 + 1))
                    if ss:
                        pe.wait_ge(v_s, q_ - 1)
                    for a_ in range(4):
                        mm = pe.matmul(bank[BC[g]][:, a_ * P:(a_ + 1) * P], feat(8, a_, g), feat(8, a_, g), start=True, stop=True)
                    mm.then_inc(p_kk, 1)
                    pe.wait_ge(a_dt, q_ + 1)
                    for a_ in range(4):
                        mm = pe.matmul(bank[BA[g]][:, a_ * P:(a_ + 1) * P], feat(8, a_, g), feat(0, a_, g), start=True, stop=True)
                    mm.then_inc(p_kk, 1)
                mod_filler(fill[1])
                for g in range(2):
                    pe.wait_ge(v_tt, 2 * ss + g + 1)
                    for a_ in range(4):
                        mm = pe.transpose(bank[BB[g]][:, a_ * P:(a_ + 1) * P], d_tt[:, g, a_], C("ident"))
                    mm.then_inc(p_x1, 1)
                for g in range(2):
                    for a_ in range(4):
                        mm = pe.matmul(bank[BC[g]][:, a_ * P:(a_ + 1) * P], feat(8, a_, g), d_s[:, g, a_], start=True, stop=True)
                    mm.then_inc(p_ks, 1)
                mod_filler(fill[2])

                def first_product(l, g):
                    for a_ in range(4):
                        mm = pe.matmul(bank[BA[g]][:, a_ * 64:a_ * 64 + 64], d_n[:, g, a_], half_cols(d_t, g, a_, LEVELS[l]),
                                       start=True, stop=True)
                    mm.then_inc(p_p, 1)

                for g in range(2):
                    pe.wait_ge(a_t1, 2 * ss + g + 1)
                    pe.wait_ge(v_at, 2 * ss + g + 1)
                    first_product(0, g)
                for l in range(len(LEVELS)):
                    for g in range(2):
                        pe.wait_ge(v_pc, lev(ss, l, g))
                        if l:
                            pe.wait_ge(a_tt, lev(ss, l - 1, g))
                        for a_ in range(4):
                            mm = pe.matmul(bank[BA[g]][:, 256 + a_ * 64:256 + a_ * 64 + 64], d_tt[:, g, a_], d_pc[:, g, a_],
                                           start=True, stop=True)
                        mm.then_inc(p_tp, 1)
                    for g in range(2):
                        pe.wait_ge(v_t, lev(ss, l, g))
                        if l + 1 < len(LEVELS):
                            first_product(l + 1, g)
                        for a_ in range(4):
                            mm = pe.transpose(bank[BB[g]][:, a_ * P:(a_ + 1) * P], d_t[:, g, a_], C("ident"))
                        mm.then_inc(p_x, 1)
                for g in range(2):
                    pe.wait_ge(a_tt, lev(ss, len(LEVELS) - 1, g))
                    pe.wait_ge(v_r, 2 * ss + g + 1)
                    for a_ in range(4):
                        mm = pe.matmul(bank[BA[g]][:, a_ * P:(a_ + 1) * P], d_tt[:, g, a_], d_r[:, g, a_], start=True, stop=True)
                    mm.then_inc(p_vn, 1)
                mod_filler(fill[3])
                for g in range(2):
                    pe.wait_ge(v_vn, 2 * ss + g + 1)
                    for a_ in range(4):
                        o_ = bank[BB[g]][:, a_ * P:(a_ + 1) * P]
                        pe.matmul(o_, d_vn[:, g, a_], d_at[:, g, a_], start=True, stop=False)
                        mm = pe.matmul(o_, d_s[:, g, a_], d_qd[:, g, a_], start=False, stop=True)
                    mm.then_inc(p_o, 1)
                    pe.wait_ge(v_vd, 2 * ss + g + 1)
                    for a_ in range(4):
                        mm = pe.matmul(bank[BC[g]][:, a_ * P:(a_ + 1) * P], k_tok[:, chunk[g] % 2, a_], d_vd[:, g, a_],
                                       start=True, stop=True)
                    mm.then_inc(p_s, 1)
                mod_filler(fill[4])
            mod_flip(5)
            sums(dnn, [T] * 8)
            pe.wait_ge(s_mix_lo, 16)
            segment(SEG["out"], mix_hi, mix_lo, 0)

            def mlp(layer, last):
                nm, n0 = f"mlp{layer}", 0 if layer == 0 else CTX
                sumsq(norm_sems[nm], T - n0)
                for half in (0, 1):
                    s_ = SEG[f"up{layer}{half}"]
                    segment(s_, h_hi, h_lo, n0, normed(nm) if half == 0 else None)
                    segment(SEG[f"down{layer}{half}"], hid_hi, hid_lo, n0,
                            lambda k: pe.wait_ge(hid_done, s_["up"] + k + 1 + PRIME_HID))

            mlp(0, False)
            sumsq(norm_sems["mix1"], T)
            segment(SEG["q"], h_hi, h_lo, CTX, normed("mix1"))
            segment(SEG["k"], h_hi, h_lo, 0)
            segment(SEG["v"], h_hi, h_lo, 0)
            sums(qkn, [T - CTX] * 8 + [T] * 4)
            pe.wait_ge(act_evac, 32)
            for h in range(4):
                if h >= 2:
                    pe.wait_ge(a_v1, h - 1)
                for n in range(NT):
                    mm = pe.transpose(bank[(X2, 3)[h % 2]][:, n * P:(n + 1) * P], v1[:, h, n * P:(n + 1) * P], C("ident"))
                mm.then_inc(p_v1, 1)
            pe.wait_ge(qkn["out"], 12)
            for i in range(6):
                if i >= 2:
                    pe.wait_ge(v_rope, i - 1)
                y_ = q1[:, 2 * i:2 * i + 2, :] if i < 4 else k1[:, 2 * i - 8:2 * i - 6, CTX:T]
                pe.matmul(bank[i % 2][:, :], C("rot"), y_, start=True, stop=True).then_inc(p_rot, 1)
            pe.wait_ge(v_rope, 6)
            pe.wait_ge(a_v1, 4)

            def scores(i):
                if i >= 2:
                    pe.wait_ge(a_ex, i - 1)
                h, qt = i // 2, i % 2
                pe.matmul(bank[i % 2][:, :], q1[:, h, qt * P:(qt + 1) * P], k1[:, h // 2], start=True, stop=True).then_inc(p_sc, 1)

            def attend(i):
                h, qt = i // 2, i % 2
                pe.wait_ge(a_pt, i + 1)
                if h >= 2 and qt == 0:
                    pe.wait_ge(v_al, h - 1)
                for n in range(NT):
                    mm = pe.matmul(bank[(X0, X1)[h % 2]][:, qt * P:(qt + 1) * P], v1_tok[:, h // 2, n], probT[:, i % 2, n],
                                   start=(n == 0), stop=(n == NT - 1))
                mm.then_inc(p_pv, 1)

            scores(0)
            for i in range(16):
                if i < 15:
                    scores(i + 1)
                pe.wait_ge(v_pr, i + 1)
                if i >= 2:
                    pe.wait_ge(a_pt, i - 1)
                for n in range(NT):
                    mm = pe.transpose(bank[2 + i % 2][:, n * P:(n + 1) * P], prob[:, i % 2, n * P:(n + 1) * P], C("ident"))
                mm.then_inc(p_pt, 1)
                if i >= 1:
                    attend(i - 1)
            attend(15)
            pe.wait_ge(v_al, 8)
            segment(SEG["wo"], att_hi, att_lo, CTX)
            mlp(1, True)
            sumsq(norm_sems["fin"], T - CTX)
            pe.wait_ge(v_y, KT)
            for i in range(4):
                for j in range(4):
                    mm = pe.transpose(bank[i][:, j * P:(j + 1) * P], y_out[:, 4 * (i % 2) + j, (i // 2) * P:(i // 2 + 1) * P],
                                      C("ident"))
                mm.then_inc(p_y, 1)


_INS = ["x", "c", "ctx", "c_ctx", "norm_mix_g", "norm_mlp_g", "w_mod", "b_mod", "mlp_w1", "mlp_w2", "even_w_in",
        "lru_conv_w", "lru_conv_b", "lru_w_a", "lru_b_a", "lru_w_i", "lru_b_i", "lru_lambda", "dn_conv_w", "dn_a_log",
        "dn_dt_bias", "dn_norm_g", "even_w_out", "attn_w_qkv", "attn_q_norm_g", "attn_k_norm_g", "attn_w_o", "final_norm_g"]


def kernel(**inputs):
    import concourse.bacc as bacc
    from concourse.bass_utils import run_bass_kernel_spmd

    nc = bacc.Bacc("TRN2", target_bir_lowering=False, num_devices=1)
    arrays, aps = {}, {}
    for name in _INS:
        arr = np.ascontiguousarray(inputs[name])
        arrays[f"in_{name}"] = arr
        aps[name] = nc.dram_tensor(f"in_{name}", arr.shape, F32, kind="ExternalInput").ap()
    arrays["in_consts"] = CONSTS
    aps["consts"] = nc.dram_tensor("in_consts", CONSTS.shape, F32, kind="ExternalInput").ap()
    out = nc.dram_tensor("out_0", (1, T - CTX, D), F32, kind="ExternalOutput").ap()
    build(nc, aps, out)
    r = run_bass_kernel_spmd(nc, [arrays], core_ids=[0])
    return r.results[0]["out_0"]
```
